# Optimizing a Trainium2 kernel written in Bass

```python
import math
import jax, jax.numpy as jnp
from jax import lax
import numpy as np

D_MODEL = 1024
BATCH = 1
SEQ = 2048
DEPTH = 1

CHUNK = 64
N_MEM = 256
HEAD_DIM = 64
N_Q_HEADS = 8
N_KV_HEADS = 2
Q_PER_KV = N_Q_HEADS // N_KV_HEADS
WINDOW = 128
WINDOW_CHUNKS = WINDOW // CHUNK
ATTN_WIDTH = N_Q_HEADS * HEAD_DIM
KV_WIDTH = N_KV_HEADS * HEAD_DIM
POOL_WINDOWS = (2, 4, 8, 16)
POOL_GROUPS = len(POOL_WINDOWS)
POOL_WIDTH = D_MODEL // 2
POOL_GROUP_DIM = POOL_WIDTH // POOL_GROUPS
N_X_HEADS = 4
X_HEAD_DIM = D_MODEL // 8
X_WIDTH = N_X_HEADS * X_HEAD_DIM
N_BRANCHES = 3
IN_WIDTH = ATTN_WIDTH + 2 * KV_WIDTH + POOL_WIDTH + X_WIDTH
D_FF = 4 * D_MODEL
EPS = 1e-6
NEG_INF = -1e30

kernel_name = "gated_hybrid_window_pool_memory_block"

def _rmsnorm(x, g):
    xf = x.astype(jnp.float32)
    y = xf * lax.rsqrt(jnp.mean(xf * xf, axis=-1, keepdims=True) + EPS)
    return (y * g.astype(jnp.float32)).astype(x.dtype)

def _alibi_slopes(n_heads):
    return jnp.exp2(-8.0 * jnp.arange(1, n_heads + 1, dtype=jnp.float32) / n_heads)

def _chunk_band(t, nc):
    b, _, h, d = t.shape
    tb = t.reshape(b, nc, CHUNK, h, d)
    parts = [jnp.pad(tb, ((0, 0), (shift, 0), (0, 0), (0, 0), (0, 0)))[:, :nc]
             for shift in range(WINDOW_CHUNKS - 1, -1, -1)]
    return jnp.concatenate(parts, axis=2)

def _window_attention(q, k, v, sinks):
    b, s = q.shape[:2]
    nc = s // CHUNK
    nk = WINDOW_CHUNKS * CHUNK
    qb = q.reshape(b, nc, CHUNK, N_KV_HEADS, Q_PER_KV, HEAD_DIM)
    kb = _chunk_band(k, nc)
    vb = _chunk_band(v, nc)
    scores = jnp.einsum('bnqgrd,bnkgd->bngrqk', qb, kb).astype(jnp.float32) * (HEAD_DIM ** -0.5)
    chunk_start = jnp.arange(nc) * CHUNK
    q_pos = chunk_start[:, None] + jnp.arange(CHUNK)[None, :]
    k_pos = chunk_start[:, None] - (WINDOW_CHUNKS - 1) * CHUNK + jnp.arange(nk)[None, :]
    dist = jnp.abs(q_pos[:, :, None] - k_pos[:, None, :]).astype(jnp.float32)
    valid = jnp.broadcast_to((k_pos >= 0)[:, None, :], dist.shape)
    slopes = _alibi_slopes(N_Q_HEADS).reshape(1, 1, N_KV_HEADS, Q_PER_KV, 1, 1)
    scores = scores - slopes * dist[None, :, None, None]
    scores = jnp.where(valid[None, :, None, None], scores, NEG_INF)
    sink = jnp.broadcast_to(sinks.astype(jnp.float32).reshape(1, 1, N_KV_HEADS, Q_PER_KV, 1, 1),
                            scores.shape[:-1] + (1,))
    probs = jax.nn.softmax(jnp.concatenate([scores, sink], axis=-1), axis=-1)[..., :-1]
    out = jnp.einsum('bngrqk,bnkgd->bnqgrd', probs.astype(v.dtype), vb)
    return out.reshape(b, s, ATTN_WIDTH)

def _multiscale_pool(u, w_pool, pool_scale):
    b, s, _ = u.shape
    ug = u.reshape(b, s, POOL_GROUPS, POOL_GROUP_DIM).astype(jnp.float32)
    csum = jnp.pad(jnp.cumsum(ug, axis=1), ((0, 0), (1, 0), (0, 0), (0, 0)))
    t = jnp.arange(s)
    outs = []
    for gi, w in enumerate(POOL_WINDOWS):
        start = jnp.maximum(t + 1 - w, 0)
        win_sum = csum[:, t + 1, gi] - csum[:, start, gi]
        cnt = (t + 1 - start).astype(jnp.float32)
        outs.append(win_sum / cnt[None, :, None] - ug[:, :, gi])
    pooled = jnp.stack(outs, axis=2).astype(u.dtype)
    mixed = jnp.einsum('bsgc,gcd->bsgd', pooled, w_pool)
    return mixed.reshape(b, s, POOL_WIDTH) * pool_scale

def _memory_attention(qx, mem_k, mem_v):
    b, s = qx.shape[:2]
    scores = jnp.einsum('bshd,bmhd->bhsm', qx, mem_k).astype(jnp.float32) * (X_HEAD_DIM ** -0.5)
    probs = jax.nn.softmax(scores, axis=-1).astype(mem_v.dtype)
    return jnp.einsum('bhsm,bmhd->bshd', probs, mem_v).reshape(b, s, X_WIDTH)

def setup_inputs(seed: int = 0) -> dict:
    key = jax.random.key(seed)
    ks = jax.random.split(key, 20)
    f32 = jnp.float32

    def nrm(k, shape, fan_in):
        return jax.random.normal(k, shape, f32) * (fan_in ** -0.5)

    def gain(k, shape):
        return 1.0 + 0.02 * jax.random.normal(k, shape, f32)

    return {
        "x": jax.random.normal(ks[0], (BATCH, SEQ, D_MODEL), f32),
        "mem": jax.random.normal(ks[1], (BATCH, N_MEM, D_MODEL), f32),
        "norm_mix_g": gain(ks[2], (DEPTH, D_MODEL)),
        "norm_mem_g": gain(ks[3], (DEPTH, D_MODEL)),
        "w_in": nrm(ks[4], (DEPTH, D_MODEL, IN_WIDTH), D_MODEL),
        "attn_sinks": 0.5 * jax.random.normal(ks[5], (DEPTH, N_Q_HEADS), f32),
        "w_pool": nrm(ks[6], (DEPTH, POOL_GROUPS, POOL_GROUP_DIM, POOL_GROUP_DIM), POOL_GROUP_DIM),
        "pool_scale": gain(ks[7], (DEPTH, POOL_WIDTH)),
        "w_mem_kv": nrm(ks[8], (DEPTH, D_MODEL, 2 * X_WIDTH), D_MODEL),
        "w_branch_attn": nrm(ks[9], (DEPTH, ATTN_WIDTH, D_MODEL), ATTN_WIDTH),
        "w_branch_pool": nrm(ks[10], (DEPTH, POOL_WIDTH, D_MODEL), POOL_WIDTH),
        "w_branch_mem": nrm(ks[11], (DEPTH, X_WIDTH, D_MODEL), X_WIDTH),
        "w_gate": nrm(ks[12], (DEPTH, D_MODEL, N_BRANCHES * D_MODEL), D_MODEL),
        "b_gate": 0.02 * jax.random.normal(ks[13], (DEPTH, N_BRANCHES * D_MODEL), f32),
        "w_out": nrm(ks[14], (DEPTH, D_MODEL, D_MODEL), D_MODEL),
        "norm_mlp_g": gain(ks[15], (DEPTH, D_MODEL)),
        "w_up": nrm(ks[16], (DEPTH, D_MODEL, D_FF), D_MODEL),
        "w_down": nrm(ks[17], (DEPTH, D_FF, D_MODEL), D_FF),
        "norm_final_g": gain(ks[18], (D_MODEL,)),
    }

def reference(x, mem, norm_mix_g, norm_mem_g, w_in, attn_sinks, w_pool, pool_scale, w_mem_kv,
              w_branch_attn, w_branch_pool, w_branch_mem, w_gate, b_gate, w_out,
              norm_mlp_g, w_up, w_down, norm_final_g):
    b, s, _ = x.shape
    m = mem.shape[1]
    for layer in range(DEPTH):
        h = _rmsnorm(x, norm_mix_g[layer])
        proj = h @ w_in[layer]
        o = 0
        q_a = proj[..., o:o + ATTN_WIDTH].reshape(b, s, N_Q_HEADS, HEAD_DIM); o += ATTN_WIDTH
        k_a = proj[..., o:o + KV_WIDTH].reshape(b, s, N_KV_HEADS, HEAD_DIM); o += KV_WIDTH
        v_a = proj[..., o:o + KV_WIDTH].reshape(b, s, N_KV_HEADS, HEAD_DIM); o += KV_WIDTH
        u_p = proj[..., o:o + POOL_WIDTH]; o += POOL_WIDTH
        q_x = proj[..., o:o + X_WIDTH].reshape(b, s, N_X_HEADS, X_HEAD_DIM)

        y_attn = _window_attention(q_a, k_a, v_a, attn_sinks[layer])
        y_pool = _multiscale_pool(u_p, w_pool[layer], pool_scale[layer])
        mkv = _rmsnorm(mem, norm_mem_g[layer]) @ w_mem_kv[layer]
        mem_k = mkv[..., :X_WIDTH].reshape(b, m, N_X_HEADS, X_HEAD_DIM)
        mem_v = mkv[..., X_WIDTH:].reshape(b, m, N_X_HEADS, X_HEAD_DIM)
        y_mem = _memory_attention(q_x, mem_k, mem_v)

        gates = jax.nn.sigmoid((h @ w_gate[layer] + b_gate[layer]).astype(jnp.float32))
        gates = gates.astype(x.dtype).reshape(b, s, N_BRANCHES, D_MODEL)
        merged = (gates[:, :, 0] * (y_attn @ w_branch_attn[layer])
                  + gates[:, :, 1] * (y_pool @ w_branch_pool[layer])
                  + gates[:, :, 2] * (y_mem @ w_branch_mem[layer]))
        x = x + merged @ w_out[layer]

        hm = _rmsnorm(x, norm_mlp_g[layer])
        x = x + jnp.square(jax.nn.relu(hm @ w_up[layer])) @ w_down[layer]
    return _rmsnorm(x, norm_final_g)


_drawn_inputs = setup_inputs


def setup_inputs(seed=0):
    import zlib

    import numpy as np

    out = dict(_drawn_inputs(seed))
    spreads = {}
    factors = {'norm_mix_g': 5.168,
     'norm_mem_g': 8.0,
     'attn_sinks': 8.0,
     'pool_scale': 17.467,
     'b_gate': 8.0,
     'norm_mlp_g': 14.234,
     'norm_final_g': 8.449}
    for name, (base, spread) in spreads.items():
        noise = np.random.default_rng([zlib.crc32(name.encode()), seed]).standard_normal(out[name].shape)
        drawn = base * np.exp(spread * noise) if base else spread * noise
        out[name] = __import__('jax').numpy.asarray(drawn.astype(out[name].dtype))
    for name, factor in factors.items():
        out[name] = (out[name] * factor).astype(out[name].dtype)
    return out
```

```python
import concourse.bass as bass
from concourse import mybir
from concourse.alu_op_type import AluOpType as ALU

F32 = mybir.dt.float32
F32R = mybir.dt.float32r
ACT = mybir.ActivationFunctionType
AX_X = mybir.AxisListType.X

P = 128
D = 1024
KT = D // P
SEQ = 2048
TB = 512
NBLK = SEQ // TB
TT = TB // P
CHUNK = 64
HD = 64
NQ = 8
NKV = 2
WIN_KEYS = 3 * CHUNK
GROUPS = 4
POOL_WINDOWS = (2, 4, 8, 16)
PAD = 16
NXH = 4
NMEM = 256
MT = NMEM // P
EPS = 1e-6
FAR = 1e30
PC = 256
ATT_SCALE = HD ** -0.5
MEM_SCALE = P ** -0.5
SLOPES = [2.0 ** (-8.0 * (h + 1) / NQ) for h in range(NQ)]

W_KV, W_Q, W_U, W_GATE0, W_POOL, W_GATE1 = 0, 1, 3, 7, 9, 10
W_MERGE, W_OUT, W_MLP = 16, 32, 36
PIECES = 68
PIECES0 = 4
G_K, G_V, G_Q, G_VT, G_UX, G_GATE0, G_POOL, G_GATE1 = 0, 1, 2, 6, 8, 16, 20, 24
G_MERGE, G_OUT, G_MLP, G_LAST = 36, 68, 84, 132
TILES = 156
G0_MEM, G0_K, G0_X, G0_V, TILES0 = 0, 4, 8, 16, 20
ATT = 4
REST = [[(4 * g + 3, 0, WIN_KEYS, 2, g * 256), (4 * g + 2, P, CHUNK, 2, g * 256 + WIN_KEYS)] for g in range(NKV)]
SCORE_PARTS = REST[0] + [(4 * g + r, 0, WIN_KEYS if r < 2 else P, g, r * WIN_KEYS) for g in range(NKV) for r in range(3)] \
    + REST[1]
LAST_STEPS = "o0a o0b o1a o1b x4 x5 x6 x7 o2a o2b o3a o3b".split()
LAST_STEPS_DVE = "n0 n1 o0 o1 x4 x5 x6 x7 n2 n3 o2 o3".split()
OUT_HALVES = [w for w in LAST_STEPS if w[0] == "o"]
HALF = NQ // 2


def mem_step(j):
    return (W_GATE0, G_GATE0) if j == 0 else (W_GATE1 + 2 * (j - 1), G_GATE1 + 4 * (j - 1))


def place(t, last):
    return t + (t - 8) // 2 if last and t >= 8 else t


def next_tile(k):
    return G_LAST + (10 + 3 * k if k < 4 else 16 + k)


def build(nc, a, out):
    off = [16512]

    def at(name, shape, dt, offset):
        return nc.alloc_sbuf_tensor_at(name, shape, dt, offset=offset)

    def sb(name, shape, dt=F32):
        size = 4
        for s in shape[1:]:
            size *= s
        t = at(name, shape, dt, off[0])
        off[0] += (size + 31) // 32 * 32
        return t

    KB = 1024
    stage = sb("stage", [P, 2, KT, PC])
    w_hi = sb("w_hi", [P, 2, KT, PC], F32R)
    w_lo = sb("w_lo", [P, 2, KT, PC], F32R)
    h_hi = sb("h_hi", [P, KT, TB], F32R)
    h_lo = sb("h_lo", [P, KT, TB], F32R)
    arena = off[0]
    off[0] += 80 * KB
    y0_hi = at("y0_hi", [P, 4, TB], F32R, arena)
    y0_lo = at("y0_lo", [P, 4, TB], F32R, arena + 8 * KB)
    xres = at("xres", [P, 2, TT, PC], F32, arena)
    out_tm = at("out_tm", [P, 2, D], F32, arena)
    q_att = at("q_att", [P, 4, TB], F32, arena + 16 * KB)
    resid = at("resid", [P, KT, TB], F32, arena + 16 * KB)
    scores = at("scores", [P, NQ, WIN_KEYS], F32, arena + 32 * KB)
    pt_a = at("pt_a", [P, NQ, P], F32, arena + 38 * KB)
    pt_b = at("pt_b", [HD, NQ, P], F32, arena + 42 * KB)
    y1_hi = at("y1_hi", [P, 4, TB], F32R, arena + 32 * KB)
    y1_lo = at("y1_lo", [P, 4, TB], F32R, arena + 40 * KB)
    q_mem = at("q_mem", [P, NXH, TB], F32, arena + 48 * KB)
    m_scores = at("m_scores", [P, NXH, NMEM], F32, arena + 56 * KB)
    m_pt = at("m_pt", [P, NXH, MT, P], F32, arena + 60 * KB)
    win_sum = at("win_sum", [P, GROUPS, PAD + TB], F32, arena + 64 * KB)
    win_tmp = at("win_tmp", [P, PAD + TB], F32, arena + 64 * KB + 8704)
    y2_hi = at("y2_hi", [P, 4, TB], F32R, arena + 64 * KB)
    y2_lo = at("y2_lo", [P, 4, TB], F32R, arena + 72 * KB)
    u_hi = at("u_hi", [P, KT, TB], F32R, arena + 32 * KB)
    u_lo = at("u_lo", [P, KT, TB], F32R, arena + 48 * KB)
    x_tm = at("x_tm", [P, TT, D], F32, arena + 64 * KB)
    m_hi = at("m_hi", [P, KT, NMEM], F32R, arena)
    m_lo = at("m_lo", [P, KT, NMEM], F32R, arena + 8 * KB)
    mem_tm = at("mem_tm", [P, MT, D], F32, arena + 16 * KB)
    rows = at("rows", [52, P], F32, arena + 32 * KB)

    mem_k = sb("mem_k", [P, NXH, NMEM])
    mem_v = sb("mem_v", [P, MT, 4 * P])
    temp = sb("temp", [P, 4, TB])
    sq = sb("sq", [P, 2, TB])
    sq_sum = sb("sq_sum", [P, TB])
    inv_rms = sb("inv_rms", [P, TB])
    u_pad = sb("u_pad", [P, GROUPS, PAD + TB])
    k_pad = sb("k_pad", [P, CHUNK + TB])
    v_pad = sb("v_pad", [P, CHUNK + TB])
    v_tm = sb("v_tm", [P, TT + 1, P])
    dist0 = sb("dist0", [P, WIN_KEYS])
    dist = sb("dist", [P, WIN_KEYS])
    g_fin = sb("g_fin", [P, D])
    ident = sb("ident", [P, P])
    ones = sb("ones", [P, P])
    par = sb("par", [P, 52])
    half_bg = sb("half_bg", [P, 24])
    sink = sb("sink", [P, NQ])
    sink8 = sb("sink8", [P, NQ])
    mx = sb("mx", [P, NQ])
    mx2 = sb("mx2", [P, NQ])
    nb = sb("nb", [P, NQ])
    sn = sb("sn", [P, NQ])
    es = sb("es", [P, NQ])
    den = sb("den", [P, NQ])
    den2 = sb("den2", [P, NQ])
    rd = sb("rd", [P, NQ])
    inv_cnt = sb("inv_cnt", [P, GROUPS, PAD])
    pos = sb("pos", [P, PAD])
    head = sb("head", [P, GROUPS, PAD])
    m_half = sb("m_half", [P, 4])
    ssum = sb("ssum", [P, 4])
    svar = sb("svar", [P, 4])
    srs = sb("srs", [P, 4])
    fsum = sb("fsum", [P, TT, 2])
    fvar = sb("fvar", [P, 4])
    frs = sb("frs", [P, 4])
    flag = sb("flag", [P, 1])
    assert off[0] <= 229344, off[0]
    PM_MIX, PM_MLP, PM_MEM, PM_BG, PM_PS = 0, 8, 16, 24, 48

    ps = nc.alloc_psum_tensor("ps", [P, 8, 512], F32)

    def sem(name):
        return nc.alloc_semaphore(name)

    const_ld = sem("const_ld")
    row_ld = sem("row_ld")
    mem_ld = sem("mem_ld")
    x_ld = sem("x_ld")
    xres_ld = [sem("xres_ld0"), sem("xres_ld1")]
    w_ld = [sem("w_ld0"), sem("w_ld1")]
    out_st = [sem("out_st0"), sem("out_st1")]
    stored = sem("stored")
    hi_done = sem("hi_done")
    lo_done = sem("lo_done")
    tile_done = sem("tile_done")
    emptied = [sem(f"emptied{i}") for i in range(4)]
    att_done = sem("att_done")
    rest_done = sem("rest_done")
    misc_done = sem("misc_done")
    setup = sem("setup")
    par_rdy = sem("par_rdy")
    d = sem("d")
    tails = sem("tails")
    sums = sem("sums")
    var_rdy = sem("var_rdy")
    rms_rdy = sem("rms_rdy")
    xn_rdy = sem("xn_rdy")
    half_hi = sem("half_hi")
    nb_rdy = sem("nb_rdy")
    ex_done = sem("ex_done")
    p_rdy = sem("p_rdy")
    pt_rdy = sem("pt_rdy")
    y_hi_done = sem("y_hi_done")
    y_done = sem("y_done")
    win = sem("win")
    pooled = sem("pooled")
    pooled_hi = sem("pooled_hi")
    pooled_lo = sem("pooled_lo")
    sum_rdy = sem("sum_rdy")
    mrg_hi = sem("mrg_hi")
    mrg_lo = sem("mrg_lo")
    sq_rdy = sem("sq_rdy")
    sq_add = sem("sq_add")
    nvar_rdy = sem("nvar_rdy")
    nrms_rdy = sem("nrms_rdy")
    diag_rdy = sem("diag_rdy")
    hm_hi = sem("hm_hi")
    hm_lo = sem("hm_lo")
    inv_rdy = sem("inv_rdy")
    u_hi_done = sem("u_hi_done")
    u_sq = sem("u_sq")
    u_lo_done = sem("u_lo_done")
    fin_tile = sem("fin_tile")
    fin_done = sem("fin_done")
    fsq = sem("fsq")
    fvar_rdy = sem("fvar_rdy")
    frms_rdy = sem("frms_rdy")

    def kp(w):
        return w.rearrange("(k p) n -> p k n", p=P)

    w_in = a["w_in"][0]
    w_q = w_in[:, 0:512].rearrange("(k p) (g tc) -> p k g tc", p=P, g=NKV)
    w_inv, w_gate, w_outv = kp(w_in), kp(a["w_gate"][0]), kp(a["w_out"][0])
    w_upv, w_downv, w_mkv = kp(a["w_up"][0]), kp(a["w_down"][0]), kp(a["w_mem_kv"][0])
    w_br = [kp(a[n][0]) for n in ("w_branch_attn", "w_branch_pool", "w_branch_mem")]
    w_poolv = a["w_pool"][0].rearrange("g c d -> c g d")
    x_rows = a["x"][0].rearrange("(t p) n -> p t n", p=P)
    out_rows = out[0].rearrange("(t p) n -> p t n", p=P)
    ring = ps

    def per_row(t, n, m):
        return t[:, 0:n].rearrange("p (h o) -> p h o", o=1).broadcast_to([P, n, m])

    def by_head(t, slot, tile, paired):
        if paired:
            return t[:, slot, :, tile * P:(tile + 1) * P].rearrange("p k (g c) -> p k g c", g=NKV)
        return t[:, slot, :, :].rearrange("p k (g c) -> p k g c", g=NKV)[:, :, :, tile * HD:(tile + 1) * HD]

    block = nc.Block()
    with block:

        @block.sync
        def _(sp):
            sp.dma_start(mem_tm[:], a["mem"][0].rearrange("(t p) n -> p t n", p=P)).then_inc(mem_ld, 16)
            for r0, n, name in ((PM_MIX, 8, "norm_mix_g"), (PM_MLP, 8, "norm_mlp_g"), (PM_MEM, 8, "norm_mem_g"),
                                (PM_BG, 24, "b_gate"), (PM_PS, 4, "pool_scale")):
                sp.dma_start(rows[r0:r0 + n, :], a[name][0].rearrange("(r c) -> r c", c=P)).then_inc(row_ld, 16)

            def load(slot, src, value=None, kt=KT, dst=None):
                if value is not None:
                    sp.wait_ge(lo_done, value)
                half = kt // 2
                if dst is None:
                    dst = (stage[:, slot, 0:half, :], stage[:, slot, half:kt, :])
                    src = (src[:, 0:half, :], src[:, half:kt, :])
                for to, part in zip(dst, src):
                    sp.dma_start(to, part).then_inc(w_ld[slot], 16)

            for n in range(PIECES0):
                load(n % 2, w_mkv[:, :, n * PC:(n + 1) * PC], n - 1 if n >= 2 else None)
                if n == 1:
                    sp.dma_start(x_tm[:], x_rows[:, 0:TT, :]).then_inc(x_ld, 16)
                    sp.dma_start(sink[:], a["attn_sinks"][0:1, :].broadcast_to([P, NQ])).then_inc(const_ld, 16)
                    sp.dma_start(g_fin[:], a["norm_final_g"].rearrange("(o n) -> o n", o=1).broadcast_to([P, D]))\
                        .then_inc(const_ld, 16)

            def load_q(n, value):
                load((W_Q + n) % 2, [w_q[:, :, g, n * 128:(n + 1) * 128] for g in range(NKV)], value,
                     dst=[stage[:, (W_Q + n) % 2, :, g * 128:(g + 1) * 128] for g in range(NKV)])

            with sp.Fori(0, NBLK) as b:
                lo0 = sp.snap(b * PIECES + (PIECES0 - 1))
                t0 = sp.snap(b * TILES + TILES0)
                row_q = sp.snap(b * TT)
                row_n = sp.snap(((b + 1) % NBLK) * TT)
                load(0, w_inv[:, :, 2 * PC:3 * PC], lo0)
                for n in range(2):
                    load_q(n, lo0 + (W_Q + n))
                for n in range(W_U, W_GATE0):
                    load(n % 2, w_inv[:, :, n * PC:(n + 1) * PC], lo0 + n)
                for j in range(4):
                    n = mem_step(j)[0]
                    load(n % 2, w_gate[:, :, j * PC:(j + 1) * PC], lo0 + n)
                    load((n + 1) % 2, w_br[0][:, :, j * PC:(j + 1) * PC], lo0 + (n + 1), kt=4)
                    if j == 0:
                        load(W_POOL % 2, [w_poolv[:, 0:2, :], w_poolv[:, 2:4, :]], lo0 + W_POOL,
                             dst=[stage[:, W_POOL % 2, k, :].rearrange("p (g c) -> p g c", g=2) for k in range(2)])
                for j in range(4):
                    cols = slice(j * PC, (j + 1) * PC)
                    base = lo0 + (W_MERGE + 4 * j)
                    load(0, w_gate[:, :, D + j * PC:D + (j + 1) * PC], base)
                    load(1, w_gate[:, :, 2 * D + j * PC:2 * D + (j + 1) * PC], base + 1)
                    load(0, w_br[1][:, :, cols], base + 2, kt=4)
                    load(1, w_br[2][:, :, cols], base + 3, kt=4)
                for j in range(4):
                    load(j % 2, w_outv[:, :, j * PC:(j + 1) * PC], lo0 + (W_OUT + j))
                    sp.wait_ge(tile_done, t0 + (G_MERGE if j < 2 else G_OUT + 4 * (j - 2) + 2))
                    sp.wait_ge(x_ld, 16)
                    sp.dma_start(xres[:, j % 2], x_rows[:, bass.ds(row_q, TT), j * PC:(j + 1) * PC])\
                        .then_inc(xres_ld[j % 2], 16)
                sp.wait_ge(tile_done, t0 + G_OUT)
                sp.wait_ge(x_ld, 16)
                sp.dma_start(x_tm[:], x_rows[:, bass.ds(row_n, TT), :]).then_inc(x_ld, 16)
                with sp.Fori(0, 4) as c:
                    base = sp.snap(lo0 + (c * 8 + W_MLP))
                    f0 = sp.snap(c * D)
                    k0 = sp.snap(c * KT)
                    for i in range(4):
                        fi = sp.snap(f0 + i * PC)
                        load(i % 2, w_upv[:, :, bass.ds(fi, PC)], base + i)
                    for i in range(4):
                        load(i % 2, w_downv[:, bass.ds(k0, KT), i * PC:(i + 1) * PC], base + (4 + i))
            load(0, w_inv[:, :, 2 * PC:3 * PC], NBLK * PIECES + PIECES0 - 1)
            load_q(0, NBLK * PIECES + PIECES0)
            for s in range(2):
                sp.wait_ge(w_ld[s], 32 * ((PIECES0 + NBLK * PIECES) // 2 + 1))

        @block.scalar
        def _(act):
            def op(*args, **kw):
                return nc.scalar.activation(*args, **kw)

            def split(slot, loads, before, kt=KT, query=False):
                act.wait_ge(w_ld[slot], loads)
                if before is not None:
                    act.wait_ge(tile_done, before)
                if query:
                    for t in range(2):
                        last = op(by_head(w_hi, slot, t, True), by_head(stage, slot, t, False), ACT.Copy)
                    last.then_inc(hi_done, 1)
                    return
                op(w_hi[:, slot, 0:kt, :], stage[:, slot, 0:kt, :], ACT.Copy).then_inc(hi_done, 1)

            def row_sums(src, t, value):
                if value is not None:
                    act.wait_ge(sums, value)
                op(sq[:].rearrange("p a n -> p (a n)"), src[:, t, :], ACT.Square,
                   accum_out=ssum[:, t:t + 1]).then_inc(sums, 1)

            act.wait_ge(mem_ld, 16)
            for t in range(MT):
                row_sums(mem_tm, t, t if t else None)
            split(0, 32, None)
            act.wait_ge(par_rdy, 1)
            op(fsum[:, :, 0], par[:, 0:TT], ACT.Copy).then_inc(fsq, 1)
            for k in range(KT):
                act.wait_ge(tile_done, G0_MEM + k // 2 + 1)
                op(m_hi[:, k, :], ring[:, k // 2, (k % 2) * NMEM:(k % 2 + 1) * NMEM], ACT.Copy,
                   scale=par[:, PM_MEM + k:PM_MEM + k + 1]).then_inc(half_hi, 1)
            split(1, 32, None)
            act.wait_ge(x_ld, 16)
            act.wait_ge(var_rdy, 1)
            for t in range(TT):
                row_sums(x_tm, t, MT + t)

            def mem_tiles(n):
                for z in range(2):
                    q = (G0_K if n < 2 else G0_V - 4) + 2 * n + z
                    act.wait_ge(tile_done, q + 1)
                    dst = mem_k[:, 2 * n + z, :] if n < 2 else mem_v[:, z, (n - 2) * PC:(n - 1) * PC]
                    op(dst, ring[:, q % 4, 0:PC], ACT.Copy).then_inc(emptied[q % 4], 1)

            mem_tiles(0)
            split(0, 64, G0_K + 2)
            mem_tiles(1)
            for k in range(KT):
                act.wait_ge(tile_done, G0_X + k + 1)
                op(h_hi[:, k, :], ring[:, k % 4, :], ACT.Copy,
                   scale=par[:, PM_MIX + k:PM_MIX + k + 1]).then_inc(half_hi, 1)
            split(1, 64, G0_X)
            mem_tiles(2)
            split(0, 96, G0_V + 2)
            mem_tiles(3)
            split(1, 96, TILES0, query=True)

            with act.Fori(0, NBLK) as b:
                t0 = act.snap(b * TILES + TILES0)
                e0 = act.snap(b * (TILES // 4) + TILES0 // 4)
                b8 = act.snap(b * 8)
                b12 = act.snap(b * 12)
                att0 = act.snap(b * 28)
                ld0 = act.snap(b * (32 * PIECES // 2) + 32 * (PIECES0 // 2 + 1))

                def hi(n, before, kt=KT, query=False):
                    split(n % 2, ld0 + 32 * (n // 2), t0 + before, kt, query)

                def copy(dst, q, src=None):
                    act.wait_ge(tile_done, t0 + (q + 1))
                    op(dst, ring[:, q % 4, :] if src is None else src, ACT.Copy).then_inc(emptied[q % 4], 1)

                op(k_pad[:, 0:CHUNK], k_pad[:, TB:TB + CHUNK], ACT.Copy)
                op(v_pad[:, 0:CHUNK], v_pad[:, TB:TB + CHUNK], ACT.Copy)
                op(u_pad[:, :, 0:PAD], u_pad[:, :, TB:TB + PAD], ACT.Copy).then_inc(tails, 1)
                act.wait_ge(tails, b + 1)
                copy(k_pad[:, CHUNK:], G_K)
                copy(v_pad[:, CHUNK:], G_V)
                hi(W_Q + 1, G_Q, query=True)
                for t in range(4):
                    if t == 2:
                        hi(W_U, G_Q + 2)
                    copy(q_att[:, t, :], G_Q + t)
                copy(v_tm[:, 0:TT, :].rearrange("p t n -> p (t n)"), G_VT)
                copy(v_tm[0:CHUNK, TT, :], G_VT + 1, ring[0:CHUNK, (G_VT + 1) % 4, 0:P])

                for i in range(TT):
                    n = W_U + i
                    hi(n + 1, G_UX + 2 * i)
                    for f in range(2):
                        act.wait_ge(nb_rdy, b12 + (2 * i + f + 1))
                        for h in range(f * HALF, (f + 1) * HALF):
                            op(scores[:, h, :], scores[:, h, :], ACT.Exp, scale=ATT_SCALE,
                               bias=nb[:, h:h + 1], accum_out=den[:, h:h + 1])
                        op(es[:, f * HALF:(f + 1) * HALF], sn[:, f * HALF:(f + 1) * HALF], ACT.Exp)\
                            .then_inc(ex_done, 1)
                    to = u_pad[:, :, PAD:] if i < 2 else q_mem
                    copy(to[:, 2 * i % 4, :], G_UX + 2 * i)
                    for f in range(2):
                        hs = slice(f * HALF, (f + 1) * HALF)
                        act.wait_ge(att_done, att0 + (4 * i + f + 2))
                        op(pt_a[:, hs, :].rearrange("p h n -> p (h n)"), ps[:, ATT + f, :], ACT.Copy)
                        last = op(pt_b[:, hs, :].rearrange("p h n -> p (h n)"), ps[0:HD, ATT + 2 + f, :], ACT.Copy)
                    last.then_inc(pt_rdy, 1)
                    copy(to[:, 2 * i % 4 + 1, :], G_UX + 2 * i + 1)
                    act.wait_ge(att_done, att0 + (4 * i + 4))
                    if i == 0:
                        act.wait_ge(stored, b + 1)
                    op(y0_hi[:, :, i * P:(i + 1) * P], ps[:, ATT + 3, :].rearrange("p (t n) -> p t n", n=P),
                       ACT.Copy).then_inc(y_hi_done, 1)

                for j in range(4):
                    n, q0 = mem_step(j)
                    if j == 1:
                        for g in range(GROUPS):
                            act.wait_ge(tile_done, t0 + (G_POOL + g + 1))
                            op(y1_hi[:, g, :], ring[:, g, :], ACT.Copy,
                               scale=par[:, PM_PS + g:PM_PS + g + 1]).then_inc(half_hi, 1)
                    hi(n + 1, q0, kt=4)
                    act.wait_ge(nb_rdy, b12 + (2 * TT + j + 1))
                    for h in range(NXH):
                        last = op(m_scores[:, h, :], ps[:, ATT + h // 2, (h % 2) * NMEM:(h % 2 + 1) * NMEM],
                                  ACT.Exp, scale=MEM_SCALE, bias=nb[:, h:h + 1], accum_out=den[:, h:h + 1])
                    last.then_inc(ex_done, 1)
                    for z in range(2):
                        if j == 0 and z == 1:
                            act.wait_ge(pooled, b + 1)
                            for g in range(GROUPS):
                                op(y1_hi[:, g, :], win_sum[:, g, PAD:], ACT.Copy).then_inc(pooled_hi, 1)
                        q = q0 + z
                        act.wait_ge(emptied[2 + z], e0 + q // 4)
                        act.wait_ge(tile_done, t0 + (q + 1))
                        op(temp[:, z, :], ring[:, z, :], ACT.Tanh, scale=0.5,
                           bias=half_bg[:, 2 * j + z:2 * j + z + 1]).then_inc(emptied[z], 1)
                    hi(n + 2, q0 + 2, kt=2 if n + 2 == W_POOL else KT)
                    act.wait_ge(att_done, att0 + (3 * j + 18))
                    for z in range(2):
                        last = op(m_pt[:, 2 * z:2 * z + 2].rearrange("p h m n -> p (h m n)"), ps[:, ATT + 2 + z, :],
                                  ACT.Copy)
                    last.then_inc(pt_rdy, 1)
                    if j == 0:
                        hi(W_GATE1, G_GATE0 + 4)
                        act.wait_ge(pooled_lo, b * 4 + 4)
                    act.wait_ge(att_done, att0 + (3 * j + 19))
                    op(y2_hi[:, :, j * P:(j + 1) * P], ps[:, ATT + 2, :].rearrange("p (t n) -> p t n", n=P),
                       ACT.Copy).then_inc(y_hi_done, 1)

                for z in range(2):
                    act.wait_ge(emptied[2 + z], e0 + G_MERGE // 4)
                with act.Fori(0, 4) as j:
                    qj = act.snap(t0 + (j * 8 + G_MERGE))
                    ldj = act.snap(ld0 + (j * 64 + 32 * (W_MERGE // 2)))
                    sj = act.snap(b * 16 + j * 4)
                    for g in range(2):
                        split(1 - g, ldj + 32 * g, qj + 2 * g, kt=KT if g == 0 else 4)
                        for z in range(2):
                            if z == 0:
                                act.wait_ge(sum_rdy, sj + 1)
                            act.wait_ge(tile_done, qj + (2 * g + z + 1))
                            op(temp[:, 2 * g + z, :], ring[:, 2 * g + z, :], ACT.Tanh, scale=0.5,
                               bias=half_bg[:, bass.ds(j * 2 + (8 * (g + 1) + z), 1)])\
                                .then_inc(emptied[2 * g + z], 1)
                    split(1, ldj + 32, qj + 4, kt=4)
                    split(0, ldj + 64, qj + 6)

                act.wait_ge(tile_done, t0 + (G_OUT - 2))
                for m in range(KT):
                    act.wait_ge(sum_rdy, b * 16 + (4 * (m // 2) + 4 + m % 2))
                    op(u_hi[:, m, :], resid[:, m, :], ACT.Copy, scale=0.5).then_inc(mrg_hi, 1)
                for j in range(4):
                    hi(W_OUT + 1 + j, G_OUT + 4 * j)
                    for z in range(2):
                        m = 2 * j + z
                        act.wait_ge(mrg_lo, b8 + (m + 1))
                        copy(resid[:, m, :], G_OUT + 4 * j + z)
                    for z in range(2):
                        m = 2 * j + z
                        act.wait_ge(emptied[2 + z], e0 + (G_OUT // 4 + j + 1))
                        op(h_hi[:, m, :], resid[:, m, :], ACT.Copy, scale=par[:, PM_MLP + m:PM_MLP + m + 1])\
                            .then_inc(hm_hi, 1)
                        if m >= 2:
                            act.wait_ge(sq_add, b8 + (m - 1))
                        op(sq[:, z, :], resid[:, m, :], ACT.Square).then_inc(sq_rdy, 1)

                def next_hi(k):
                    q = next_tile(k)
                    act.wait_ge(tile_done, t0 + (q + 1))
                    op(h_hi[:, k, :], ring[:, q % 4, :], ACT.Copy,
                       scale=par[:, PM_MIX + k:PM_MIX + k + 1]).then_inc(half_hi, 1)

                def mlp_chunk(qc, ec, ldc, first=False, last=False):
                    for i in range(4):
                        split(1 - i % 2, ldc + 32 * ((i + 1) // 2), qc + 2 * i)
                        for t in (2 * i, 2 * i + 1):
                            act.wait_ge(emptied[t % 4], ec + (t // 4 + 1))
                            op(u_hi[:, t, :], temp[:, t % 2, :], ACT.Square).then_inc(u_hi_done, 1)
                        if first and i >= 2:
                            act.wait_ge(x_ld, b * 16 + 32)
                            act.wait_ge(inv_rdy, b + 1)
                            for t in (2 * i - 4, 2 * i - 3):
                                row_sums(x_tm, t, b * 4 + (MT + TT + t))
                    for i in range(4):
                        split(1 - i % 2, ldc + 32 * ((i + 5) // 2), qc + (place(7 + 2 * i, last) + 1))
                        if last:
                            next_hi(i)

                mlp_chunk(t0 + G_MLP, e0 + G_MLP // 4, ld0 + 32 * (W_MLP // 2), first=True)
                with act.Fori(1, 3) as c:
                    mlp_chunk(act.snap(t0 + (c * 16 + G_MLP)), act.snap(e0 + (c * 4 + G_MLP // 4)),
                              act.snap(ld0 + (c * 128 + 32 * (W_MLP // 2))))
                mlp_chunk(t0 + G_LAST, e0 + G_LAST // 4, ld0 + (3 * 128 + 32 * (W_MLP // 2)), last=True)

                for step in LAST_STEPS:
                    if step[0] == "x":
                        next_hi(int(step[1]))
                    else:
                        t, z, i = int(step[1]), "ab".index(step[2]), OUT_HALVES.index(step)
                        act.wait_ge(fsq, b8 + (i + 1))
                        act.wait_ge(fin_tile, b8 + (i + 1))
                        op(sq[:, z, :], ps[:, ATT + 2 * (t % 2) + z, :], ACT.Square,
                           accum_out=fsum[:, t, z:z + 1]).then_inc(fsq, 1)
                hi(PIECES + 1, next_tile(3), query=True)

        @block.vector
        def _(dve):
            v = nc.vector

            def low(slot, value, kt=KT, query=False):
                dve.wait_ge(hi_done, value)
                if query:
                    for t in range(2):
                        last = v.tensor_tensor(by_head(w_lo, slot, t, True), by_head(stage, slot, t, False),
                                               by_head(w_hi, slot, t, True).bitcast(F32), ALU.subtract)
                    last.then_inc(lo_done, 1)
                    return
                v.tensor_tensor(w_lo[:, slot, 0:kt, :], stage[:, slot, 0:kt, :], w_hi[:, slot, 0:kt, :].bitcast(F32),
                                ALU.subtract).then_inc(lo_done, 1)

            dve.wait_ge(setup, 1)
            v.scalar_tensor_tensor(out=dist[:], in0=dist0[:], scalar=-1.0, in1=dist0[:], op0=ALU.mult, op1=ALU.max)\
                .then_inc(d, 1)
            for g, w in enumerate(POOL_WINDOWS):
                v.tensor_scalar(inv_cnt[:, g, :], pos[:], float(w), None, ALU.min).then_inc(d, 1)
            dve.wait_ge(d, 5)
            v.reciprocal(inv_cnt[:], inv_cnt[:]).then_inc(fin_done, 1)
            v.memset(dist[0:CHUNK, 2 * CHUNK:], FAR).then_inc(y_done, 1)
            v.memset(dist[CHUNK:P, 0:CHUNK], FAR).then_inc(d, 1)
            dve.wait_ge(d, 6)
            v.tensor_copy(dist0[:], dist[:]).then_inc(d, 1)
            dve.wait_ge(d, 7)
            v.memset(dist0[0:CHUNK, 0:CHUNK], FAR).then_inc(d, 1)
            dve.wait_ge(misc_done, 1)
            v.tensor_copy(par[:], ps[:, 6, 0:52]).then_inc(d, 1)
            dve.wait_ge(d, 9)
            v.tensor_scalar(half_bg[:], par[:, PM_BG:PM_BG + 24], 0.5, None, ALU.mult).then_inc(par_rdy, 1)

            def norm_rows(tm, nt, done, before):
                dve.wait_ge(sums, done)
                v.tensor_scalar(svar[:, 0:nt], ssum[:, 0:nt], D * EPS, None, ALU.add).then_inc(var_rdy, 1)
                dve.wait_ge(rms_rdy, before + 1)
                for t in range(nt):
                    last = v.tensor_scalar(tm[:, t, :], tm[:, t, :], srs[:, t:t + 1], float(D) ** 0.5,
                                           ALU.mult, ALU.mult)
                last.then_inc(xn_rdy, 1)

            def low_rows(k, src, g0, dst, hi_src, value, sem_):
                dve.wait_ge(half_hi, value)
                return v.scalar_tensor_tensor(out=dst, in0=src, scalar=par[:, g0 + k:g0 + k + 1],
                                              in1=hi_src.bitcast(F32), op0=ALU.mult, op1=ALU.subtract)\
                    .then_inc(sem_, 1)

            norm_rows(mem_tm, MT, MT, 0)
            low(0, 1)
            for k in range(KT):
                low_rows(k, ring[:, k // 2, (k % 2) * NMEM:(k % 2 + 1) * NMEM], PM_MEM, m_lo[:, k, :], m_hi[:, k, :],
                         k // 2 * 2 + 2, emptied[k // 2] if k % 2 else d)
            low(1, 2)
            norm_rows(x_tm, TT, MT + TT, 1)
            low(0, 3)
            for k in range(KT):
                low_rows(k, ring[:, k % 4, :], PM_MIX, h_lo[:, k, :], h_hi[:, k, :], KT + k + 1, emptied[k % 4])
            low(1, 4)
            dve.wait_ge(const_ld, 32)
            v.tensor_scalar(sink8[:], sink[:], 1.0 / ATT_SCALE, None, ALU.mult).then_inc(d, 1)
            v.tensor_scalar(g_fin[:], g_fin[:], float(D) ** 0.5, None, ALU.mult).then_inc(d, 1)
            low(0, 5)
            low(1, 6, query=True)
            d0 = 15

            D_BLK = 59
            with dve.Fori(0, NBLK) as b:
                t0 = dve.snap(b * TILES + TILES0)
                e0 = dve.snap(b * (TILES // 4) + TILES0 // 4)
                b8 = dve.snap(b * 8)
                b12 = dve.snap(b * 12)
                att0 = dve.snap(b * 28)
                p0 = dve.snap(b * PIECES + PIECES0)
                dd = dve.snap(b * D_BLK + d0)
                step = [0]

                def chained(ins):
                    ins.then_inc(d, 1)
                    step[0] += 1
                    dve.wait_ge(d, dd + step[0])

                def lo(n, kt=KT, query=False):
                    low(n % 2, p0 + (n + 1), kt, query)

                lo(W_Q + 1, query=True)
                lo(W_U)
                for i in range(TT):
                    n = W_U + i
                    dve.wait_ge(att_done, att0 + (4 * i + 1))
                    dst_ = dist0 if i == 0 else dist
                    for f in range(2):
                        hs = slice(f * HALF, (f + 1) * HALF)
                        for h, k0, n_, bank, col in SCORE_PARTS:
                            if h // HALF == f:
                                last = v.scalar_tensor_tensor(
                                    out=scores[:, h, k0:k0 + n_], in0=dst_[:, k0:k0 + n_],
                                    scalar=-SLOPES[h] / ATT_SCALE, in1=ps[:, ATT + bank, col:col + n_],
                                    op0=ALU.mult, op1=ALU.add)
                        chained(last)
                        chained(v.tensor_reduce(mx[:, hs], scores[:, hs, :], AX_X, ALU.max))
                        chained(v.tensor_tensor(mx2[:, hs], mx[:, hs], sink8[:, hs], ALU.max))
                        chained(v.tensor_scalar(nb[:, hs], mx2[:, hs], -ATT_SCALE, None, ALU.mult))
                        v.tensor_tensor(sn[:, hs], sink[:, hs], nb[:, hs], ALU.add).then_inc(nb_rdy, 1)
                    if i == 0:
                        v.tensor_copy(dist0[:], dist[:]).then_inc(d, 1)
                        step[0] += 1
                    for f in range(2):
                        hs = slice(f * HALF, (f + 1) * HALF)
                        dve.wait_ge(ex_done, b12 + (2 * i + f + 1))
                        chained(v.tensor_tensor(den2[:, hs], den[:, hs], es[:, hs], ALU.add))
                        chained(v.reciprocal(rd[:, hs], den2[:, hs]))
                        v.tensor_tensor(scores[:, hs, :], scores[:, hs, :],
                                        rd[:, hs].rearrange("p (h o) -> p h o", o=1).broadcast_to([P, HALF, WIN_KEYS]),
                                        ALU.mult).then_inc(p_rdy, 1)
                    lo(n + 1)
                    dve.wait_ge(y_hi_done, b8 + (i + 1))
                    v.tensor_tensor(y0_lo[:, :, i * P:(i + 1) * P],
                                    ps[:, ATT + 3, :].rearrange("p (t n) -> p t n", n=P),
                                    y0_hi[:, :, i * P:(i + 1) * P].bitcast(F32), ALU.subtract).then_inc(y_done, 1)

                for j in range(4):
                    n, q0 = mem_step(j)
                    if j == 1:
                        for g in range(GROUPS):
                            low_rows(g, ring[:, g, :], PM_PS, y1_lo[:, g, :], y1_hi[:, g, :],
                                     b * 12 + (2 * KT + g + 1), emptied[g])
                    dve.wait_ge(att_done, att0 + (3 * j + 17))
                    chained(v.tensor_reduce(mx[:, 0:NXH], ps[:, ATT:ATT + 2, :].rearrange("p a (h n) -> p (a h) n", h=2),
                                            AX_X, ALU.max))
                    v.tensor_scalar(nb[:, 0:NXH], mx[:, 0:NXH], -MEM_SCALE, None, ALU.mult).then_inc(nb_rdy, 1)
                    lo(n + 1, kt=4)
                    dve.wait_ge(ex_done, b12 + (2 * TT + j + 1))
                    chained(v.reciprocal(rd[:, 0:NXH], den[:, 0:NXH]))
                    v.tensor_tensor(m_scores[:], m_scores[:], per_row(rd, NXH, NMEM), ALU.mult).then_inc(p_rdy, 1)
                    if j == 0:
                        dve.wait_ge(win, b * 10 + 11)
                        chained(v.tensor_tensor(head[:], win_sum[:, :, PAD:2 * PAD], inv_cnt[:], ALU.mult))
                        for g, w in enumerate(POOL_WINDOWS):
                            v.scalar_tensor_tensor(out=win_sum[:, g, PAD:], in0=win_sum[:, g, PAD:], scalar=1.0 / w,
                                                   in1=u_pad[:, g, PAD:], op0=ALU.mult, op1=ALU.subtract)
                            last = v.memset(inv_cnt[:, g, :], 1.0 / w)
                        chained(last)
                        v.tensor_tensor(win_sum[:, :, PAD:2 * PAD], head[:], u_pad[:, :, PAD:2 * PAD], ALU.subtract)\
                            .then_inc(pooled, 1)
                        for g in range(GROUPS):
                            dve.wait_ge(pooled_hi, b * 4 + (g + 1))
                            v.tensor_tensor(y1_lo[:, g, :], win_sum[:, g, PAD:], y1_hi[:, g, :].bitcast(F32),
                                            ALU.subtract).then_inc(pooled_lo, 1)
                    lo(n + 2, kt=2 if n + 2 == W_POOL else KT)
                    for z in range(2):
                        q = q0 + 2 + z
                        dve.wait_ge(emptied[z], e0 + (q // 4 + 1))
                        dve.wait_ge(tile_done, t0 + (q + 1))
                        v.scalar_tensor_tensor(out=resid[:, 2 * j + z, :], in0=temp[:, z, :], scalar=1.0,
                                               in1=ring[:, 2 + z, :], op0=ALU.add, op1=ALU.mult)\
                            .then_inc(emptied[2 + z], 1)
                    if j == 0:
                        lo(W_GATE1)
                    dve.wait_ge(y_hi_done, b8 + (j + 5))
                    v.tensor_tensor(y2_lo[:, :, j * P:(j + 1) * P], ps[:, ATT + 2, :].rearrange("p (t n) -> p t n", n=P),
                                    y2_hi[:, :, j * P:(j + 1) * P].bitcast(F32), ALU.subtract).then_inc(y_done, 1)

                with dve.Fori(0, 4) as j:
                    qj = dve.snap(t0 + (j * 8 + G_MERGE))
                    ej = dve.snap(e0 + (j * 2 + G_MERGE // 4))
                    pj = dve.snap(p0 + (j * 4 + W_MERGE))
                    low(1, pj + 2)
                    low(0, pj + 3, kt=4)
                    low(1, pj + 4, kt=4)
                    for g in range(2):
                        for z in range(2):
                            dve.wait_ge(emptied[2 * g + z], ej + 1)
                            dve.wait_ge(tile_done, qj + (4 + 2 * g + z + 1))
                            v.scalar_tensor_tensor(out=temp[:, 2 * g + z, :], in0=temp[:, 2 * g + z, :], scalar=1.0,
                                                   in1=ring[:, 2 * g + z, :], op0=ALU.add, op1=ALU.mult)\
                                .then_inc(emptied[2 * g + z], 1)
                        if g == 0:
                            low(0, pj + 5)

                for m in range(KT):
                    dve.wait_ge(mrg_hi, b8 + (m + 1))
                    v.scalar_tensor_tensor(out=u_lo[:, m, :], in0=resid[:, m, :], scalar=0.5,
                                           in1=u_hi[:, m, :].bitcast(F32), op0=ALU.mult, op1=ALU.subtract)\
                        .then_inc(mrg_lo, 1)
                for j in range(4):
                    lo(W_OUT + 1 + j)
                    for z in range(2):
                        m = 2 * j + z
                        q = G_OUT + 4 * j + 2 + z
                        dve.wait_ge(emptied[z], e0 + (q // 4 + 1))
                        dve.wait_ge(tile_done, t0 + (q + 1))
                        v.tensor_tensor(resid[:, m, :], resid[:, m, :], ring[:, 2 + z, :], ALU.add)\
                            .then_inc(emptied[2 + z], 1)
                    for z in range(2):
                        m = 2 * j + z
                        dve.wait_ge(hm_hi, b8 + (m + 1))
                        v.scalar_tensor_tensor(out=h_lo[:, m, :], in0=resid[:, m, :],
                                               scalar=par[:, PM_MLP + m:PM_MLP + m + 1],
                                               in1=h_hi[:, m, :].bitcast(F32), op0=ALU.mult, op1=ALU.subtract)\
                            .then_inc(hm_lo, 1)

                def next_lo(k):
                    q = next_tile(k)
                    low_rows(k, ring[:, q % 4, :], PM_MIX, h_lo[:, k, :], h_hi[:, k, :],
                             b * 12 + (2 * KT + 4 + k + 1), emptied[q % 4])

                def mlp_chunk(qc, ec, pc, uc, first=False, last=False):
                    for i in range(4):
                        low(1 - i % 2, pc + (i + 2))
                        if first and i == 0:
                            dve.wait_ge(misc_done, b * 2 + 2)
                            v.tensor_scalar(fvar[:], ps[:, ATT, 0:TT], D * EPS, None, ALU.add).then_inc(nvar_rdy, 1)
                            dve.wait_ge(nrms_rdy, b + 1)
                            for t in range(TT):
                                ins = v.tensor_scalar(sq[:, 0, t * P:(t + 1) * P], ident[:], frs[:, t:t + 1],
                                                      float(D) ** 0.5, ALU.mult, ALU.mult)
                            ins.then_inc(diag_rdy, 1)
                            dve.wait_ge(misc_done, b * 2 + 3)
                            v.tensor_copy(inv_rms[:], ps[:, ATT + 1, :]).then_inc(inv_rdy, 1)
                            dve.wait_ge(inv_rdy, b + 1)
                        for t in (2 * i, 2 * i + 1):
                            dve.wait_ge(tile_done, qc + (t + 1))
                            v.scalar_tensor_tensor(out=temp[:, t % 2, :], in0=ring[:, t % 4, :], scalar=0.0,
                                                   in1=inv_rms[:], op0=ALU.max, op1=ALU.mult)\
                                .then_inc(emptied[t % 4], 1)
                            dve.wait_ge(emptied[t % 4], ec + (t // 4 + 1))
                            v.tensor_tensor(temp[:, 2 + t % 2, :], temp[:, t % 2, :], temp[:, t % 2, :], ALU.mult)\
                                .then_inc(u_sq, 1)
                            dve.wait_ge(u_sq, uc + (t + 1))
                            dve.wait_ge(u_hi_done, uc + (t + 1))
                            v.tensor_tensor(u_lo[:, t, :], temp[:, 2 + t % 2, :], u_hi[:, t, :].bitcast(F32),
                                            ALU.subtract).then_inc(u_lo_done, 1)
                    if first:
                        norm_rows(x_tm, TT, b * 4 + (MT + 2 * TT), b + 2)
                    for i in range(4):
                        low(1 - i % 2, pc + (i + 6))
                        for z in range(2):
                            t = place(8 + 2 * i + z, last)
                            dve.wait_ge(tile_done, qc + (t + 1))
                            v.tensor_tensor(resid[:, 2 * i + z, :], resid[:, 2 * i + z, :], ring[:, t % 4, :],
                                            ALU.add).then_inc(emptied[t % 4], 1)
                        if last:
                            next_lo(i)

                mlp_chunk(t0 + G_MLP, e0 + G_MLP // 4, p0 + W_MLP, b * 32, first=True)
                with dve.Fori(1, 3) as c:
                    mlp_chunk(dve.snap(t0 + (c * 16 + G_MLP)), dve.snap(e0 + (c * 4 + G_MLP // 4)),
                              dve.snap(p0 + (c * 8 + W_MLP)), dve.snap(b * 32 + c * 8))
                mlp_chunk(t0 + G_LAST, e0 + G_LAST // 4, p0 + (W_MLP + 24), b * 32 + 24, last=True)

                for what, n in LAST_STEPS_DVE:
                    if what == "x":
                        next_lo(int(n))
                        continue
                    t = int(n)
                    if what == "n":
                        dve.wait_ge(fsq, b8 + (OUT_HALVES.index(f"o{t}b") + 2))
                        v.tensor_scalar(fvar[:, t:t + 1], fsum[:, t, 0:1], fsum[:, t, 1:2], D * EPS, ALU.add, ALU.add)\
                            .then_inc(fvar_rdy, 1)
                        continue
                    dve.wait_ge(frms_rdy, b * 4 + (t + 1))
                    if t < 2:
                        dve.wait_ge(stored, b + 1)
                    else:
                        dve.wait_ge(out_st[t % 2], b * 32 + 16)
                    for z in range(2):
                        last = v.scalar_tensor_tensor(
                            out=out_tm[:, t % 2, z * 512:(z + 1) * 512], in0=ps[:, ATT + 2 * (t % 2) + z, :],
                            scalar=frs[:, t:t + 1], in1=g_fin[:, z * 512:(z + 1) * 512],
                            op0=ALU.mult, op1=ALU.mult)
                    last.then_inc(fin_done, 1)
                lo(PIECES + 1, query=True)
                assert step[0] == D_BLK, step[0]

        @block.gpsimd
        def _(pool):
            g_ = nc.gpsimd
            g_.memset(ident[:], 0.0).then_inc(win, 1)
            g_.memset(ones[:], 1.0)
            g_.memset(m_half[:], -0.5).then_inc(sum_rdy, 1)
            g_.memset(k_pad[:, TB:], 0.0).then_inc(stored, 1)
            g_.memset(v_pad[:, TB:], 0.0)
            g_.memset(u_pad[:, :, TB:], 0.0)
            g_.iota(dist0[:], [[-1, WIN_KEYS]], base=CHUNK, channel_multiplier=1,
                    allow_small_or_imprecise_dtypes=True)
            g_.iota(pos[:], [[1, PAD]], base=1, channel_multiplier=0, allow_small_or_imprecise_dtypes=True)
            pool.wait_ge(win, 1)
            g_.affine_select(out=ident[:], in_=ident[:], compare_op=ALU.not_equal, fill=1.0, base=0,
                             pattern=[[-1, P]], channel_multiplier=1).then_inc(setup, 1)

            def power(dst, src, n, wait_sem, value, done):
                pool.wait_ge(wait_sem, value)
                g_.tensor_tensor(dst, src, m_half[:, 0:n], ALU.pow).then_inc(done, 1)

            power(srs[:, 0:MT], svar[:, 0:MT], MT, var_rdy, 1, rms_rdy)
            power(srs[:], svar[:], TT, var_rdy, 2, rms_rdy)

            with pool.Fori(0, NBLK) as b:
                e0 = pool.snap(b * (TILES // 4) + TILES0 // 4)
                b8 = pool.snap(b * 8)
                b16 = pool.snap(b * 16)
                w0 = pool.snap(b * 10 + 1)
                for z in range(4):
                    pool.wait_ge(emptied[z], e0 + (G_UX // 4 + 1))
                steps = 0
                for g in range(GROUPS):
                    src = u_pad[:, g, :]
                    for s in range(g + 1):
                        dst = win_sum[:, g, :] if (g - s) % 2 == 0 else win_tmp[:]
                        sh, first = 2 ** s, 2 ** (s + 1) - 1
                        if steps:
                            pool.wait_ge(win, w0 + steps)
                        g_.tensor_tensor(dst[:, first:], src[:, first:], src[:, first - sh:PAD + TB - sh], ALU.add)\
                            .then_inc(win, 1)
                        steps += 1
                        src = dst

                for j in range(4):
                    ej = e0 + (j * 2 + G_MERGE // 4)
                    sj = b16 + j * 4
                    for g in range(2):
                        for z in range(2):
                            if g:
                                pool.wait_ge(sum_rdy, sj + (z + 2))
                            else:
                                pool.wait_ge(emptied[2 + z], e0 + G_MERGE // 4)
                            pool.wait_ge(emptied[2 * g + z], ej + 2)
                            dst = resid[:, 2 * j + z, :]
                            g_.tensor_tensor(dst, dst, temp[:, 2 * g + z, :], ALU.add).then_inc(sum_rdy, 1)

                for m in range(KT):
                    pool.wait_ge(sq_rdy, b8 + (m + 1))
                    if m == 1:
                        g_.tensor_tensor(sq_sum[:], sq[:, 0, :], sq[:, 1, :], ALU.add).then_inc(sq_add, 2)
                    elif m > 1:
                        pool.wait_ge(sq_add, b8 + m)
                        g_.tensor_tensor(sq_sum[:], sq_sum[:], sq[:, m % 2, :], ALU.add).then_inc(sq_add, 1)
                power(frs[:], fvar[:], TT, nvar_rdy, b + 1, nrms_rdy)
                power(srs[:], svar[:], TT, var_rdy, b + 3, rms_rdy)
                for t in range(TT):
                    for u in (t, t + 1) if t % 2 == 0 else ():
                        power(frs[:, u:u + 1], fvar[:, u:u + 1], 1, fvar_rdy, b * 4 + (u + 1), frms_rdy)
                    pool.wait_ge(fin_done, b * 4 + (t + 2))
                    pool.dma_start(out_rows[:, bass.ds(b * TT + t, 1), :].rearrange("p t n -> p (t n)"), out_tm[:, t % 2, :])\
                        .then_inc(out_st[t % 2], 16)
                for s in range(2):
                    pool.wait_ge(out_st[s], b * 32 + 32)
                g_.tensor_tensor(flag[:], m_half[:, 0:1], m_half[:, 0:1], ALU.add).then_inc(stored, 1)
            for s in range(2):
                pool.wait_ge(out_st[s], 32 * NBLK)

        @block.tensor
        def _(pe):
            mm = nc.tensor.matmul

            def product(dst, wh, wl, xh, xl, first, last):
                mm(dst, wh, xh, start=first, stop=False)
                mm(dst, wh, xl, start=False, stop=False)
                return mm(dst, wl, xh, start=False, stop=last)

            def transpose(dst, src, n=P):
                return nc.tensor.transpose(dst, src, ident[0:n, 0:n])

            pe.wait_ge(setup, 1)
            pe.wait_ge(row_ld, 80)
            transpose(ps[:, 6, 0:52], rows[:], 52).then_inc(misc_done, 1)
            pe.wait_ge(xn_rdy, 1)
            for q in range(4):
                for z in range(2):
                    for t in range(MT):
                        k = 2 * q + z
                        last = transpose(ring[:, q, z * NMEM + t * P:z * NMEM + (t + 1) * P],
                                         mem_tm[:, t, k * P:(k + 1) * P])
                last.then_inc(tile_done, 1)
            for n in range(PIECES0):
                if n == 2:
                    pe.wait_ge(xn_rdy, 2)
                    for k in range(KT):
                        q = G0_X + k
                        pe.wait_ge(emptied[q % 4], q // 4)
                        for t in range(TT):
                            last = transpose(ring[:, q % 4, t * P:(t + 1) * P], x_tm[:, t, k * P:(k + 1) * P])
                        last.then_inc(tile_done, 1)
                s = n % 2
                pe.wait_ge(lo_done, n + 1)
                for z in range(2):
                    q = (G0_K if n < 2 else G0_V - 4) + 2 * n + z
                    for k in range(KT):
                        if n == z == 0:
                            pe.wait_ge(emptied[k // 2], 1)
                        elif k == 0:
                            pe.wait_ge(emptied[q % 4], q // 4)
                        c = slice(z * P, (z + 1) * P)
                        wh, wl = w_hi[:, s, k, :], w_lo[:, s, k, :]
                        xh, xl = m_hi[:, k, :], m_lo[:, k, :]
                        if n < 2:
                            last = product(ring[:, q % 4, 0:PC], wh[:, c], wl[:, c], xh, xl, k == 0, k == KT - 1)
                        else:
                            last = product(ring[:, q % 4, 0:PC], xh[:, c], xl[:, c], wh, wl, k == 0, k == KT - 1)
                    last.then_inc(tile_done, 1)

            with pe.Fori(0, NBLK) as b:
                e0 = pe.snap(b * (TILES // 4) + TILES0 // 4)
                b8 = pe.snap(b * 8)
                b12 = pe.snap(b * 12)
                b4 = pe.snap(b * 4)
                p0 = pe.snap(b * PIECES + PIECES0)

                def gemm(slot, z, bank, xh, xl, kt=KT, ready=None):
                    for k in range(kt):
                        if ready is not None:
                            ready(k)
                        wh, wl = w_hi[:, slot, k, z * P:(z + 1) * P], w_lo[:, slot, k, z * P:(z + 1) * P]
                        last = product(ring[:, bank, :], wh, wl, xh[:, k, :], xl[:, k, :], k == 0, k == kt - 1)
                    last.then_inc(tile_done, 1)

                def piece(n, q0, xh, xl, kt=KT, ready=None, between=None):
                    pe.wait_ge(lo_done, p0 + (n + 1))
                    for z in range(2):
                        q = q0 + z
                        pe.wait_ge(emptied[q % 4], e0 + q // 4)
                        gemm(n % 2, z, q % 4, xh, xl, kt, between if z else ready)

                piece(W_KV, G_K, h_hi, h_lo, ready=lambda k: pe.wait_ge(
                    emptied[next_tile(k) % 4], e0 + (next_tile(k) // 4 + 1 - TILES // 4)))
                for n in range(2):
                    piece(W_Q + n, G_Q + 2 * n, h_hi, h_lo)
                pe.wait_ge(emptied[G_V], e0 + 1)
                for z in range(2):
                    pe.wait_ge(emptied[G_VT % 4 + z], e0 + G_VT // 4)
                for t in range(TT):
                    last = transpose(ring[:, G_VT % 4, t * P:(t + 1) * P], v_pad[:, t * P:(t + 1) * P])
                last.then_inc(tile_done, 1)
                transpose(ring[0:CHUNK, G_VT % 4 + 1, 0:P], v_pad[:, TB:TB + CHUNK]).then_inc(tile_done, 1)

                for i in range(TT):
                    if i == 0:
                        for q in range(G_Q, G_Q + 4):
                            pe.wait_ge(emptied[q % 4], e0 + (q // 4 + 1))
                        pe.wait_ge(fin_done, b * 4 + 1)
                    for h, k0, n_, bank, col in SCORE_PARTS:
                        g, t = h // 4, h % 4
                        if (h, k0, n_, bank, col) == REST[1][0]:
                            pe.wait_ge(rest_done, b4 + (i + 1))
                        last = mm(ps[:, ATT + bank, col:col + n_], q_att[g * HD:(g + 1) * HD, t, i * P:(i + 1) * P],
                                  k_pad[g * HD:(g + 1) * HD, i * P + k0:i * P + k0 + n_], start=True, stop=True)
                        if (h, k0, n_, bank, col) == REST[0][1]:
                            last.then_inc(rest_done, 1)
                    last.then_inc(att_done, 1)

                    def probs_across(k):
                        f = k - 4
                        if f not in (0, 1):
                            return
                        if f == 0:
                            pe.wait_ge(y_done, b8 + (i + 1))
                        pe.wait_ge(p_rdy, b12 + (2 * i + f + 1))
                        for h in range(f * HALF, (f + 1) * HALF):
                            transpose(ps[:, ATT + h // 4, (h % 4) * P:(h % 4 + 1) * P], scores[:, h, 0:P])
                        for h in range(f * HALF, (f + 1) * HALF):
                            last = transpose(ps[0:HD, ATT + 2 + h // 4, (h % 4) * P:(h % 4 + 1) * P],
                                             scores[:, h, P:])
                        last.then_inc(att_done, 1)

                    piece(W_U + i, G_UX + 2 * i, h_hi, h_lo, between=probs_across)
                    pe.wait_ge(pt_rdy, b8 + (i + 1))
                    if i == 0:
                        for z in range(2):
                            pe.wait_ge(emptied[G_VT % 4 + z], e0 + (G_VT // 4 + 1))
                    for h in range(NQ):
                        g = h // 4
                        o = ps[(h % 2) * HD:(h % 2 + 1) * HD, ATT + 3, (h // 2) * P:(h // 2 + 1) * P]
                        mm(o, v_tm[:, i, g * HD:(g + 1) * HD], pt_a[:, h, :], start=True, stop=False)
                        last = mm(o, v_tm[0:HD, i + 1, g * HD:(g + 1) * HD], pt_b[:, h, :], start=False, stop=True)
                    last.then_inc(att_done, 1)

                for j in range(4):
                    n, q = mem_step(j)
                    for h in range(NXH):
                        if j == 0:
                            pe.wait_ge(emptied[h], e0 + ((G_UX + 4) // 4 + 1))
                        last = mm(ps[:, ATT + h // 2, (h % 2) * NMEM:(h % 2 + 1) * NMEM],
                                  q_mem[:, h, j * P:(j + 1) * P], mem_k[:, h, :], start=True, stop=True)
                    last.then_inc(att_done, 1)
                    piece(n, q, h_hi, h_lo)
                    pe.wait_ge(p_rdy, b12 + (2 * TT + j + 1))
                    pe.wait_ge(y_done, b8 + (j + 5))
                    for h in range(NXH):
                        for t in range(MT):
                            c = (h % 2) * MT + t
                            last = transpose(ps[:, ATT + 2 + h // 2, c * P:(c + 1) * P],
                                             m_scores[:, h, t * P:(t + 1) * P])
                    last.then_inc(att_done, 1)
                    piece(n + 1, q + 2, y0_hi, y0_lo, kt=4)
                    pe.wait_ge(pt_rdy, b8 + (j + 5))
                    for h in range(NXH):
                        for t in range(MT):
                            last = mm(ps[:, ATT + 2, h * P:(h + 1) * P], mem_v[:, t, h * P:(h + 1) * P], m_pt[:, h, t, :],
                                      start=t == 0, stop=t == MT - 1)
                    last.then_inc(att_done, 1)
                    if j:
                        continue
                    pe.wait_ge(lo_done, p0 + (W_POOL + 1))
                    for g in range(GROUPS):
                        pe.wait_ge(pooled_lo, b * 4 + (g + 1))
                        pe.wait_ge(emptied[g], e0 + G_POOL // 4)
                        c = slice((g % 2) * P, (g % 2 + 1) * P)
                        product(ring[:, g, :], w_hi[:, W_POOL % 2, g // 2, c], w_lo[:, W_POOL % 2, g // 2, c],
                                y1_hi[:, g, :], y1_lo[:, g, :], True, True).then_inc(tile_done, 1)

                with pe.Fori(0, 4) as j:
                    ej = pe.snap(e0 + (j * 2 + G_MERGE // 4))
                    pj = pe.snap(p0 + (j * 4 + W_MERGE))
                    for r, (xh, xl, kt) in enumerate(((h_hi, h_lo, KT), (h_hi, h_lo, KT),
                                                      (y1_hi, y1_lo, 4), (y2_hi, y2_lo, 4))):
                        pe.wait_ge(lo_done, pj + (r + 1))
                        if r == 3:
                            pe.wait_ge(y_done, b8 + 9)
                        for z in range(2):
                            bank = (2 * r + z) % 4
                            pe.wait_ge(emptied[bank], ej + r // 2)
                            gemm(r % 2, z, bank, xh, xl, kt)

                for j in range(4):
                    pe.wait_ge(xres_ld[j % 2], b * 32 + (16 * (j // 2) + 16))
                    for z in range(2):
                        q = G_OUT + 4 * j + z
                        pe.wait_ge(emptied[z], e0 + q // 4)
                        for t in range(TT):
                            last = transpose(ring[:, z, t * P:(t + 1) * P], xres[:, j % 2, t, z * P:(z + 1) * P])
                        last.then_inc(tile_done, 1)
                    piece(W_OUT + j, G_OUT + 4 * j + 2, u_hi, u_lo,
                          ready=(lambda k: pe.wait_ge(mrg_lo, b8 + (k + 1))) if j == 0 else None)

                def token_sums(k):
                    if k == 5:
                        pe.wait_ge(sq_add, b8 + 8)
                        for t in range(TT):
                            last = mm(ps[:, ATT, t:t + 1], sq_sum[:, t * P:(t + 1) * P], ones[:, 0:1],
                                      start=True, stop=True)
                        last.then_inc(misc_done, 1)

                def token_rms(k):
                    if k == 3:
                        pe.wait_ge(diag_rdy, b + 1)
                        mm(ps[:, ATT + 1, :], ones[:], sq[:, 0, :], start=True, stop=True).then_inc(misc_done, 1)

                def next_rows(k):
                    q = next_tile(k)
                    pe.wait_ge(emptied[q % 4], e0 + q // 4)
                    for t in range(TT):
                        last = transpose(ring[:, q % 4, t * P:(t + 1) * P], x_tm[:, t, k * P:(k + 1) * P])
                    last.then_inc(tile_done, 1)

                def mlp_chunk(ec, pc, uc, first=False, last=False):
                    for half, (xh, xl) in enumerate(((h_hi, h_lo), (u_hi, u_lo))):
                        for i in range(4):
                            pe.wait_ge(lo_done, pc + (4 * half + i + 1))
                            for z in range(2):
                                t = 8 * half + 2 * i + z

                                def ready(k):
                                    if half and i == z == 0:
                                        pe.wait_ge(u_lo_done, uc + (k + 1))
                                    if first and t == 0:
                                        pe.wait_ge(hm_lo, b8 + (k + 1))
                                        token_sums(k)
                                    if first and t == 1:
                                        token_rms(k)

                                q = place(t, last)
                                pe.wait_ge(emptied[q % 4], ec + q // 4)
                                gemm(i % 2, z, q % 4, xh, xl, KT, ready)
                            if last and half:
                                next_rows(i)

                mlp_chunk(e0 + G_MLP // 4, p0 + W_MLP, b8 * 4, first=True)
                with pe.Fori(1, 3) as c:
                    mlp_chunk(pe.snap(e0 + (c * 4 + G_MLP // 4)), pe.snap(p0 + (c * 8 + W_MLP)),
                              pe.snap(b * 32 + c * 8))
                pe.wait_ge(xn_rdy, b + 3)
                mlp_chunk(e0 + G_LAST // 4, p0 + (W_MLP + 24), b8 * 4 + 24, last=True)

                for step in LAST_STEPS:
                    if step[0] == "x":
                        next_rows(int(step[1]))
                        continue
                    t, z = int(step[1]), "ab".index(step[2])
                    if step in ("o0a", "o0b"):
                        for q in (G_LAST + place(8 + 4 * z + m, True) for m in range(4)):
                            pe.wait_ge(emptied[q % 4], e0 + (q // 4 + 1))
                    elif t >= 2 and z == 0:
                        pe.wait_ge(fin_done, b * 4 + t)
                    for k in range(4):
                        last = transpose(ps[:, ATT + 2 * (t % 2) + z, k * P:(k + 1) * P],
                                         resid[:, 4 * z + k, t * P:(t + 1) * P])
                    last.then_inc(fin_tile, 1)


_INS = ["x", "mem", "norm_mix_g", "norm_mem_g", "w_in", "attn_sinks", "w_pool", "pool_scale", "w_mem_kv",
        "w_branch_attn", "w_branch_pool", "w_branch_mem", "w_gate", "b_gate", "w_out", "norm_mlp_g", "w_up",
        "w_down", "norm_final_g"]


def kernel(**inputs):
    import numpy as np
    import concourse.bacc as bacc
    from concourse.bass_utils import run_bass_kernel_spmd

    nc = bacc.Bacc("TRN2", target_bir_lowering=False, num_devices=1)
    arrays, aps = {}, {}
    for name in _INS:
        arrays[f"in_{name}"] = np.ascontiguousarray(inputs[name])
        aps[name] = nc.dram_tensor(f"in_{name}", arrays[f"in_{name}"].shape, F32, kind="ExternalInput").ap()
    out = nc.dram_tensor("out", (1, SEQ, D), F32, kind="ExternalOutput").ap()
    build(nc, aps, out)
    r = run_bass_kernel_spmd(nc, [arrays], core_ids=[0])
    return r.results[0]["out"]
```
